# Optimizing a Trainium2 kernel written in Bass

```python
import math, functools
import jax, jax.numpy as jnp
from jax import lax
import numpy as np

D_MODEL = 1024
BATCH = 1
SEQ = 1024
DEPTH = 1
DEC_BATCH = 1
DEC_SEQ = 32
PAST_LEN = 1024

CHUNK = 64
LEFT_CHUNKS = 8
BAND_PAST = LEFT_CHUNKS * CHUNK
BAND = BAND_PAST + CHUNK
D_ATTN = D_MODEL // 2
HEAD_DIM = 64
N_HEADS = D_ATTN // HEAD_DIM
REL_CLIP = 128
N_REL = 2 * REL_CLIP + 1
D_POOL = D_MODEL // 2
POOL_WINDOWS = (2, 4, 8, 16)
N_POOL_GRP = len(POOL_WINDOWS)
POOL_GRP = D_POOL // N_POOL_GRP
POOL_PAD = max(POOL_WINDOWS) - 1
N_BRANCH = 2
IN_COLS = D_POOL + 3 * D_ATTN + N_BRANCH * D_MODEL
D_FF = 2816
CONV_W = 3
PLE_DIM = 256
EPS = 1e-6
NEG_INF = -1e30

kernel_name = "hybrid_pool_chunkattn_streaming_encoder_step"

def rmsnorm(x, g):
    xf = x.astype(jnp.float32)
    y = xf * lax.rsqrt(jnp.mean(xf * xf, axis=-1, keepdims=True) + EPS)
    return (y * g.astype(jnp.float32)).astype(x.dtype)

def pool_mixer(u, buf, pos0, w_grp, scale):
    B, L, _ = u.shape
    full = jnp.concatenate([buf, u], axis=1)
    ff = full.astype(jnp.float32)
    cs = jnp.concatenate([jnp.zeros_like(ff[:, :1]), jnp.cumsum(ff, axis=1)], axis=1)
    pos = pos0 + jnp.arange(L, dtype=jnp.int32)
    means = []
    for g, w in enumerate(POOL_WINDOWS):
        sl = slice(g * POOL_GRP, (g + 1) * POOL_GRP)
        end = cs[:, POOL_PAD + 1:POOL_PAD + 1 + L, sl]
        start = cs[:, POOL_PAD + 1 - w:POOL_PAD + 1 - w + L, sl]
        cnt = jnp.minimum(pos + 1, w).astype(jnp.float32)[None, :, None]
        means.append((end - start) / cnt)
    d = (jnp.concatenate(means, axis=-1) - u.astype(jnp.float32)).astype(u.dtype)
    d = d.reshape(B, L, N_POOL_GRP, POOL_GRP)
    y = jnp.einsum('blgc,gcd->blgd', d, w_grp).reshape(B, L, D_POOL) * scale
    return y, full[:, -POOL_PAD:]

def band_attend(q, k, v, q_pos, k_pos, k_valid, rel_bias):
    s = jnp.einsum('bqhd,bkhd->bhqk', q, k).astype(jnp.float32) * (HEAD_DIM ** -0.5)
    rel = jnp.clip(q_pos[:, None] - k_pos[None, :], -REL_CLIP, REL_CLIP) + REL_CLIP
    s = s + rel_bias[:, rel].astype(jnp.float32)[None]
    s = jnp.where(k_valid[None, None, None, :], s, NEG_INF)
    p = jax.nn.softmax(s, axis=-1)
    return jnp.einsum('bhqk,bkhd->bqhd', p.astype(v.dtype), v)

def chunk_attention_prompt(q, k, v, rel_bias):
    B, L, H, Dh = q.shape
    n_chunks = L // CHUNK
    pad = jnp.zeros((B, BAND_PAST, H, Dh), k.dtype)
    k_pad = jnp.concatenate([pad, k], axis=1)
    v_pad = jnp.concatenate([pad, v], axis=1)

    def one_chunk(c):
        start = c * CHUNK
        q_c = lax.dynamic_slice_in_dim(q, start, CHUNK, axis=1)
        k_b = lax.dynamic_slice_in_dim(k_pad, start, BAND, axis=1)
        v_b = lax.dynamic_slice_in_dim(v_pad, start, BAND, axis=1)
        q_pos = start + jnp.arange(CHUNK, dtype=jnp.int32)
        k_pos = start - BAND_PAST + jnp.arange(BAND, dtype=jnp.int32)
        return band_attend(q_c, k_b, v_b, q_pos, k_pos, k_pos >= 0, rel_bias)

    out = lax.map(one_chunk, jnp.arange(n_chunks, dtype=jnp.int32))
    out = jnp.moveaxis(out, 0, 1).reshape(B, L, H * Dh)
    keep = min(BAND_PAST, L)
    return out, k[:, L - keep:], v[:, L - keep:]

def chunk_attention_sample(q, k, v, cache_k, cache_v, rel_bias):
    B, L, H, Dh = q.shape
    n_c = cache_k.shape[1]
    k_all = jnp.concatenate([cache_k, k], axis=1)
    v_all = jnp.concatenate([cache_v, v], axis=1)
    q_pos = PAST_LEN + jnp.arange(L, dtype=jnp.int32)
    k_pos = jnp.concatenate([PAST_LEN - n_c + jnp.arange(n_c, dtype=jnp.int32), q_pos])
    out = band_attend(q, k_all, v_all, q_pos, k_pos, k_pos >= 0, rel_bias).reshape(B, L, H * Dh)
    return out, k, v

def conv_ffn(h, buf, w_up, w_dw, b_dw, w_down):
    L = h.shape[1]
    up = h @ w_up
    a, b = jnp.split(up, 2, axis=-1)
    full = jnp.concatenate([buf, a], axis=1)
    conv = b_dw + sum(full[:, t:t + L] * w_dw[t] for t in range(CONV_W))
    y = (jax.nn.gelu(conv) * b) @ w_down
    return y, full[:, -(CONV_W - 1):]

def trunk_layer(x, p_i, pool_buf, conv_buf, pos0, attn_fn, lw):
    (g_mix, w_in, b_gate, w_pool_grp, pool_scale, w_pool_proj, w_attn_proj, w_out,
     g_ffn, w_up, w_dw, b_dw, w_down, g_ple, w_ple, w_ple_gate) = lw
    B, L, _ = x.shape
    h = rmsnorm(x, g_mix)
    z = h @ w_in
    u, q, k, v, gl = jnp.split(
        z, [D_POOL, D_POOL + D_ATTN, D_POOL + 2 * D_ATTN, D_POOL + 3 * D_ATTN], axis=-1)
    g_pool, g_attn = jnp.split(jax.nn.sigmoid(gl + b_gate), 2, axis=-1)
    pool_out, new_pool = pool_mixer(u, pool_buf, pos0, w_pool_grp, pool_scale)
    attn_out, new_k, new_v = attn_fn(q.reshape(B, L, N_HEADS, HEAD_DIM),
                                     k.reshape(B, L, N_HEADS, HEAD_DIM),
                                     v.reshape(B, L, N_HEADS, HEAD_DIM))
    merged = g_pool * (pool_out @ w_pool_proj) + g_attn * (attn_out @ w_attn_proj)
    x = x + merged @ w_out
    ffn_out, new_conv = conv_ffn(rmsnorm(x, g_ffn), conv_buf, w_up, w_dw, b_dw, w_down)
    x = x + ffn_out
    x = x + (p_i @ w_ple) * jax.nn.sigmoid(rmsnorm(x, g_ple) @ w_ple_gate)
    return x, new_pool, new_k, new_v, new_conv

def setup_inputs(seed: int = 0) -> dict:
    key = jax.random.key(seed)
    ks = jax.random.split(key, 32)

    def nrm(k, shape, scale=1.0):
        return jax.random.normal(k, shape, jnp.float32) * scale

    n_cache_att = min(BAND_PAST, PAST_LEN)
    return {
        "x_prompt": nrm(ks[0], (BATCH, SEQ, D_MODEL)),
        "x_sample": nrm(ks[1], (DEC_BATCH, DEC_SEQ, D_MODEL)),
        "cache_pool": nrm(ks[2], (DEPTH, DEC_BATCH, POOL_PAD, D_POOL)),
        "cache_k": nrm(ks[3], (DEPTH, DEC_BATCH, n_cache_att, N_HEADS, HEAD_DIM)),
        "cache_v": nrm(ks[4], (DEPTH, DEC_BATCH, n_cache_att, N_HEADS, HEAD_DIM)),
        "cache_ffn_conv": nrm(ks[5], (DEPTH, DEC_BATCH, CONV_W - 1, D_FF)),
        "p_prompt": nrm(ks[6], (DEPTH, BATCH, SEQ, PLE_DIM)),
        "p_sample": nrm(ks[7], (DEPTH, DEC_BATCH, DEC_SEQ, PLE_DIM)),
        "g_mix": 1.0 + nrm(ks[8], (DEPTH, D_MODEL), 0.02),
        "w_in": nrm(ks[9], (DEPTH, D_MODEL, IN_COLS), D_MODEL ** -0.5),
        "b_gate": nrm(ks[10], (DEPTH, N_BRANCH * D_MODEL), 0.02),
        "w_pool_grp": nrm(ks[11], (DEPTH, N_POOL_GRP, POOL_GRP, POOL_GRP), POOL_GRP ** -0.5),
        "pool_scale": 1.0 + nrm(ks[12], (DEPTH, D_POOL), 0.02),
        "rel_bias": nrm(ks[13], (DEPTH, N_HEADS, N_REL), 0.5),
        "w_pool_proj": nrm(ks[14], (DEPTH, D_POOL, D_MODEL), D_POOL ** -0.5),
        "w_attn_proj": nrm(ks[15], (DEPTH, D_ATTN, D_MODEL), D_ATTN ** -0.5),
        "w_out": nrm(ks[16], (DEPTH, D_MODEL, D_MODEL), D_MODEL ** -0.5),
        "g_ffn": 1.0 + nrm(ks[17], (DEPTH, D_MODEL), 0.02),
        "w_up": nrm(ks[18], (DEPTH, D_MODEL, 2 * D_FF), D_MODEL ** -0.5),
        "w_dw": nrm(ks[19], (DEPTH, CONV_W, D_FF), CONV_W ** -0.5),
        "b_dw": nrm(ks[20], (DEPTH, D_FF), 0.02),
        "w_down": nrm(ks[21], (DEPTH, D_FF, D_MODEL), D_FF ** -0.5),
        "g_ple": 1.0 + nrm(ks[22], (DEPTH, D_MODEL), 0.02),
        "w_ple": nrm(ks[23], (DEPTH, PLE_DIM, D_MODEL), PLE_DIM ** -0.5),
        "w_ple_gate": nrm(ks[24], (DEPTH, D_MODEL, D_MODEL), D_MODEL ** -0.5),
        "g_final": 1.0 + nrm(ks[25], (D_MODEL,), 0.02),
    }

def reference(x_prompt, x_sample, cache_pool, cache_k, cache_v, cache_ffn_conv, p_prompt, p_sample,
              g_mix, w_in, b_gate, w_pool_grp, pool_scale, rel_bias, w_pool_proj, w_attn_proj, w_out,
              g_ffn, w_up, w_dw, b_dw, w_down, g_ple, w_ple, w_ple_gate, g_final):
    xp, xs = x_prompt, x_sample
    B = xp.shape[0]
    pool_p, k_p, v_p, conv_p = [], [], [], []
    pool_s, k_s, v_s, conv_s = [], [], [], []
    for i in range(DEPTH):
        lw = (g_mix[i], w_in[i], b_gate[i], w_pool_grp[i], pool_scale[i], w_pool_proj[i],
              w_attn_proj[i], w_out[i], g_ffn[i], w_up[i], w_dw[i], b_dw[i], w_down[i],
              g_ple[i], w_ple[i], w_ple_gate[i])
        xp, a1, a2, a3, a4 = trunk_layer(
            xp, p_prompt[i],
            jnp.zeros((B, POOL_PAD, D_POOL), xp.dtype),
            jnp.zeros((B, CONV_W - 1, D_FF), xp.dtype),
            0,
            functools.partial(chunk_attention_prompt, rel_bias=rel_bias[i]),
            lw)
        pool_p.append(a1); k_p.append(a2); v_p.append(a3); conv_p.append(a4)
        xs, b1, b2, b3, b4 = trunk_layer(
            xs, p_sample[i], cache_pool[i], cache_ffn_conv[i], PAST_LEN,
            functools.partial(chunk_attention_sample, cache_k=cache_k[i], cache_v=cache_v[i],
                              rel_bias=rel_bias[i]),
            lw)
        pool_s.append(b1); k_s.append(b2); v_s.append(b3); conv_s.append(b4)
    y_prompt = rmsnorm(xp, g_final)
    y_sample = rmsnorm(xs, g_final)
    new_pool_prompt = jnp.stack(pool_p)
    new_k_prompt = jnp.stack(k_p)
    new_v_prompt = jnp.stack(v_p)
    new_conv_prompt = jnp.stack(conv_p)
    new_pool_sample = jnp.stack(pool_s)
    new_k_sample = jnp.stack(k_s)
    new_v_sample = jnp.stack(v_s)
    new_conv_sample = jnp.stack(conv_s)
    return (y_prompt, y_sample, new_pool_prompt, new_k_prompt, new_v_prompt, new_conv_prompt,
            new_pool_sample, new_k_sample, new_v_sample, new_conv_sample)


_drawn_inputs = setup_inputs


def setup_inputs(seed=0):
    import zlib

    import numpy as np

    out = dict(_drawn_inputs(seed))
    spreads = {}
    factors = {'g_mix': 2.901,
     'b_gate': 8.0,
     'pool_scale': 6.29,
     'g_ffn': 7.713,
     'b_dw': 16.109,
     'g_ple': 200.0,
     'g_final': 21.464,
     'cache_k': 6.64,
     'cache_v': 5.557,
     'p_prompt': 3.446,
     'p_sample': 3.397,
     'w_ple': 3.37,
     'w_ple_gate': 4.854}
    for name, (base, spread) in spreads.items():
        noise = np.random.default_rng([zlib.crc32(name.encode()), seed]).standard_normal(out[name].shape)
        drawn = base * np.exp(spread * noise) if base else spread * noise
        out[name] = __import__('jax').numpy.asarray(drawn.astype(out[name].dtype))
    for name, factor in factors.items():
        out[name] = (out[name] * factor).astype(out[name].dtype)
    return out
```

```python
from contextlib import ExitStack

import numpy as np

import concourse.bass as bass
from concourse import mybir

ALU = mybir.AluOpType
ACT = mybir.ActivationFunctionType
F32 = mybir.dt.float32
F32R = mybir.dt.float32r

P = 128
D_MODEL = 1024
SEQ = 1024
NEW = 32
T = SEQ + NEW
CH = 3
CW = T // CH
KT = D_MODEL // P
HEAD = 64
PAIRS = D_MODEL // 2 // P
CHUNK = 64
PAST = 512
BAND = PAST + P
QT = SEQ // P
REL_CLIP = 128
N_REL = 2 * REL_CLIP + 1
LINE = PAST + P + REL_CLIP
WINDOWS = (2, 4, 8, 16)
PAD = 16
HIST = max(WINDOWS) - 1
UW = PAD + SEQ + PAD + NEW
SAMPLE_U = PAD + SEQ + PAD
FF = 2816
FT = FF // P
GROUPS = FT // 2
AW = 2 + SEQ + 2 + NEW
SAMPLE_A = 2 + SEQ + 2
CWID = AW - 2
PLE = 256
EPS = 1e-6
SCALE = HEAD ** -0.5
MASKED = -1e30 / SCALE
BIG = 3.0e38

S_PAIR = 0
S_GATE = 4 * PAIRS
S_OUT = S_GATE + 3 * KT
S_FFN = S_OUT + KT
S_PLE = S_FFN + 6 * GROUPS
S_PGATE = S_PLE + 2
TILES = S_PGATE + KT

J_NORM1 = 1
J_Q0 = 2
J_PAIR = 3
J_FIRST = J_PAIR + 4 * PAIRS - 1
J_POOL = J_FIRST + 2
J_GATE = J_POOL + PAIRS - 2
J_OUT = J_GATE + 4 * KT
J_FFN = J_OUT + KT
J_GROUP = J_FFN + 5
J_DOWN = J_GROUP + 12 * (GROUPS - 1)
J_PLE = J_DOWN + KT
J_NORM3 = J_PLE + KT
J_PGATE = J_NORM3 + 1
J_NORM4 = J_PGATE + KT

UNITS = 2 * (QT + 1)
OTILES = QT + 1


ORDER = [7, 0, 6, 8, 1, 5, 2, 4, 3]


def blocks_of(t):
    return min(PAST // P + 1, t + 1)


def build(nc, xT, pT, w_stream, w_group, relr, g_cols, bias_cols, pool_cols, dw_cols, ckT, cv, cpoolT, cconvT,
          o_y, o_pool_p, o_pool_s, o_k, o_v, o_conv):
    ctx = ExitStack()
    with ctx:
        line_dram = nc.dram_tensor("bias_lines", (2 * PAIRS, P, LINE), F32, kind="Internal").ap()

        base = (nc.sbuf_base + 63) // 64 * 64
        TB = T * 4
        R0, R1, R2 = base, base + 16 * TB, base + 32 * TB
        R_END = R2 + 8 * TB

        def at(name, shape, dt, offset):
            return nc.alloc_sbuf_tensor_at(name, [P] + shape, dt, offset=offset)

        cursor = [R_END]

        def fixed(name, shape, dt=F32):
            t = at(name, shape, dt, cursor[0])
            cursor[0] += (int(np.prod(shape)) * 4 + 31) // 32 * 32
            return t

        w_raw = [fixed(f"w_raw{k}", [KT * P]) for k in range(2)]
        w_hi = [fixed(f"w_hi{k}", [KT * P], F32R) for k in range(2)]
        w_lo = [fixed(f"w_lo{k}", [KT * P], F32R) for k in range(2)]
        rms = fixed("rms", [T])
        acc = fixed("acc", [T])
        tmp = fixed("tmp", [UW])
        wg_raw = fixed("wg_raw", [PAIRS * P])
        wg_hi = fixed("wg_hi", [PAIRS * P], F32R)
        wg_lo = fixed("wg_lo", [PAIRS * P], F32R)
        ones = fixed("ones", [P])
        ident = fixed("ident", [P])
        g_sb = fixed("g_sb", [4 * KT])
        gate_b = fixed("gate_b", [2 * KT])
        pool_sc = fixed("pool_sc", [PAIRS])
        dw = fixed("dw", [4 * FT])
        conv_hist = fixed("conv_hist", [FT, 2])
        conv_new = fixed("conv_new", [FT, 4])
        eps = fixed("eps", [1])
        zero = fixed("zero", [1])
        gap = fixed("gap", [4])
        nmax = fixed("nmax", [4])
        rsum = fixed("rsum", [4])
        rinv = fixed("rinv", [4])
        inv_cnt = fixed("inv_cnt", [PAIRS, PAD])
        win = fixed("win", [UW])
        part = fixed("part", [UW])
        d_lo1 = fixed("d_lo1", [T], F32R)
        assert cursor[0] <= nc.sbuf_usable_end

        h1_hi = at("h1_hi", [KT, T], F32R, R0)
        h1_lo = at("h1_lo", [KT, T], F32R, R0 + 8 * TB)
        m_hi = at("m_hi", [KT, T], F32R, R0)
        m_lo = at("m_lo", [KT, T], F32R, R0 + 8 * TB)
        mid_hi = at("mid_hi", [2, T], F32R, R0)
        mid_lo = at("mid_lo", [2, T], F32R, R0 + 2 * TB)
        FW = 4352
        a_row = at("a_row", [AW], F32, R0 + 4 * TB)
        conv = at("conv", [CWID], F32, R0 + 4 * TB + FW)
        gel = at("gel", [CWID], F32, R0 + 4 * TB + 2 * FW)
        b_row = at("b_row", [T], F32, R0 + 4 * TB + 3 * FW)
        mid = at("mid", [T], F32, R0 + 4 * TB + 3 * FW + TB)
        ple = at("ple", [KT, T], F32, R0)
        gate_sb = at("gate_sb", [T], F32, R0 + 8 * TB)
        p_raw = at("p_raw", [2, T], F32, R0 + 10 * TB)
        p_hi = at("p_hi", [2, T], F32R, R0 + 12 * TB)
        p_lo = at("p_lo", [2, T], F32R, R0 + 14 * TB)
        assert 4 * TB + 3 * FW + 2 * TB <= 10 * TB
        line = at("line", [LINE], F32, R1)
        at_hi = at("at_hi", [PAIRS, T], F32R, R1)
        at_lo = at("at_lo", [PAIRS, T], F32R, R1 + 4 * TB)
        H = R1 + 8 * TB
        y_hi = at("y_hi", [PAIRS, T], F32R, H)
        y_lo = at("y_lo", [PAIRS, T], F32R, H + 4 * TB)
        qT = at("qT", [T], F32, H)
        kT = at("kT", [T], F32, H + TB)
        vT = at("vT", [T], F32, H + 2 * TB)
        v_tok = at("v_tok", [OTILES, P], F32, H + 3 * TB)
        b2 = H + 3 * TB + OTILES * P * 4
        ck_sb = at("ck_sb", [PAST], F32, b2)
        cv_sb = at("cv_sb", [PAST // P, P], F32, b2 + 2048)
        bias_sb = at("bias_sb", [2, BAND], F32, b2 + 4096)
        o_tok = at("o_tok", [P], F32, b2 + 4096 + 5120)
        s_sb = [at("s_sb0", [BAND], F32, b2 + 9728), at("s_sb1", [BAND], F32, R2 + 4 * UW * 4)]
        p_sb = [at("p_sb0", [BAND], F32, b2 + 12288), at("p_sb1", [BAND], F32, R2 + 4 * UW * 4 + 2560)]
        assert b2 + 12288 + 2560 <= R2
        pt_sb = [at(f"pt_sb{k}", [BAND], F32, R2 + 4 * UW * 4 + 5120 + 2560 * k) for k in range(2)]
        h2_hi = at("h2_hi", [KT, T], F32R, R1)
        h2_lo = at("h2_lo", [KT, T], F32R, R1 + 8 * TB)
        x_in = at("x_in", [KT, T], F32, R2)
        u_row = at("u_row", [PAIRS, UW], F32, R2)
        d_hi = [at(f"d_hi{k}", [T], F32R, R2 + 4 * UW * 4 + k * TB) for k in range(2)]
        d_lo = [at("d_lo0", [T], F32R, R2 + 4 * UW * 4 + 2 * TB), d_lo1]
        assert 4 * UW * 4 + 3 * TB <= 8 * TB
        merged = at("merged", [KT, T], F32, R2)
        x_res = at("x_res", [KT, T], F32, R2)

        ps = ctx.enter_context(nc.psum_tensor("ps", [P, 8 * 512], F32))

        def job_set(n):
            return ps[:, (n % 2) * 1536:(n % 2) * 1536 + 1536].rearrange("p (c n) -> p c n", c=CH)[:, :, 0:CW]

        def by_chunk(ap):
            return ap.rearrange("p (c n) -> p c n", c=CH)

        ps_s = [ps[:, 0:1024], ps[:, 3072:4096]]
        ps_pt = ps[:, 1536:2560]
        ps_o = ps[:, 2560:2560 + P]
        ps_ot = ps[:, 1024:1024 + P]
        ps_vt = [ps[:, 3072:3584], ps[:, 3584:4096], ps[:, 1024:1024 + P]]

        def sem(name):
            return ctx.enter_context(nc.semaphore(name))

        w_loaded = [sem("w_loaded0"), sem("w_loaded1")]
        w_hi_done = sem("w_hi_done")
        w_split = sem("w_split")
        tile_done = sem("tile_done")
        part_done = sem("part_done")
        norm_done = sem("norm_done")
        pool_done = sem("pool_done")
        evacuated = sem("evacuated")
        x_loaded = [sem(f"x_loaded{k}") for k in range(KT)]
        consts_loaded = sem("consts_loaded")
        consts_made = sem("consts_made")
        group_hi = sem("group_hi")
        group_split = sem("group_split")
        line_loaded = sem("line_loaded")
        line_made = sem("line_made")
        line_stored = sem("line_stored")
        pair_loaded = sem("pair_loaded")
        pool_hist_loaded = sem("pool_hist_loaded")
        hi_done = sem("hi_done")
        h_split = sem("h_split")
        sq_done = sem("sq_done")
        acc_done = sem("acc_done")
        root_done = sem("root_done")
        rms_ready = sem("rms_ready")
        link = sem("link")
        kv_stored = sem("kv_stored")
        vt_done = sem("vt_done")
        v_ready = sem("v_ready")
        group_loaded = sem("group_loaded")
        mask_set = sem("mask_set")
        s_done = sem("s_done")
        s_read = sem("s_read")
        p_done = sem("p_done")
        pt_done = sem("pt_done")
        pt_read = sem("pt_read")
        inv_done = sem("inv_done")
        pv_done = sem("pv_done")
        o_read = sem("o_read")
        ot_done = sem("ot_done")
        at_hi_done = sem("at_hi_done")
        at_split = sem("at_split")
        d_ready = sem("d_ready")
        d_hi_done = sem("d_hi_done")
        d_split = sem("d_split")
        y_hi_done = sem("y_hi_done")
        gate_out = sem("gate_out")
        merged_ready = sem("merged_ready")
        m_hi_done = sem("m_hi_done")
        m_split = sem("m_split")
        x_again = [sem(f"x_again{k}") for k in range(KT)]
        conv0_done = sem("conv0_done")
        conv1_done = sem("conv1_done")
        conv_done = sem("conv_done")
        gelu_done = sem("gelu_done")
        mid_ready = sem("mid_ready")
        mid_hi_done = sem("mid_hi_done")
        mid_split = sem("mid_split")
        conv_kept = sem("conv_kept")
        p_loaded = sem("p_loaded")
        p_hi_done = sem("p_hi_done")
        p_split = sem("p_split")
        gated = sem("gated")
        x4_ready = sem("x4_ready")
        y_ready = sem("y_ready")
        pool_stored = sem("pool_stored")
        stored = sem("stored")

        block = ctx.enter_context(nc.Block())

        @block.sync
        def _(sp):
            def load_tile(s, k, first=False):
                if not first:
                    sp.wait_ge(w_split, s - 1)
                sp.dma_start(w_raw[k][:], w_stream[s]).then_inc(w_loaded[k], 16)

            def load_pair(j):
                sp.dma_start(ck_sb[:], ckT[j]).then_inc(pair_loaded, 16)
                sp.dma_start(cv_sb[:], cv[j]).then_inc(pair_loaded, 16)
                sp.dma_start(bias_sb[:], bass.AP(line_dram.tensor, 2 * j * P * LINE + P - 1,
                                                 [[LINE - 1, P], [P * LINE, 2], [1, BAND]])).then_inc(pair_loaded, 16)

            sp.dma_start(g_sb[:], g_cols).then_inc(consts_loaded, 16)
            sp.dma_start(x_in[:, 0, :], xT[0]).then_inc(x_loaded[0], 16)
            load_tile(0, 0, first=True)
            sp.dma_start(line[0:2 * PAIRS, LINE - N_REL:LINE], relr).then_inc(line_loaded, 16)
            for k in range(1, KT):
                sp.dma_start(x_in[:, k, :], xT[k]).then_inc(x_loaded[k], 16)
            load_tile(1, 1, first=True)
            for dst, src in ((gate_b[:], bias_cols), (pool_sc[:], pool_cols), (dw[:], dw_cols),
                             (conv_hist[:], cconvT)):
                sp.dma_start(dst, src).then_inc(consts_loaded, 16)
            sp.dma_start(wg_raw[:], w_group).then_inc(group_loaded, 16)
            sp.wait_ge(h_split, KT)
            sp.wait_ge(sq_done, KT)
            for g in range(PAIRS):
                sp.dma_start(u_row[:, g, SAMPLE_U - HIST:SAMPLE_U], cpoolT[g]).then_inc(pool_hist_loaded, 16)
            sp.wait_ge(line_stored, 16)
            load_pair(0)
            load_tile(2, 0)
            load_tile(3, 1)
            with sp.Fori(1, PAIRS) as j:
                load_tile(4 * j, 0)
                load_tile(4 * j + 1, 1)
                sp.wait_ge(s_read, UNITS * j)
                sp.wait_ge(pv_done, UNITS * j)
                load_pair(j)
                load_tile(4 * j + 2, 0)
                load_tile(4 * j + 3, 1)
            with sp.Fori(S_GATE // 2, TILES // 2) as i:
                load_tile(2 * i, 0)
                load_tile(2 * i + 1, 1)

        n_consts = 4 + sum(WINDOWS)

        @block.gpsimd
        def _(pool):
            def split(s, i, k, first=False):
                pool.wait_ge(w_loaded[k], 16 * i + 16)
                if not first:
                    pool.wait_ge(tile_done, s - 1)
                pool.tensor_tensor(w_hi[k][:], w_raw[k][:], zero[:].broadcast_to([P, KT * P]), ALU.add).then_inc(w_hi_done, 1)
                pool.wait_ge(w_hi_done, s + 1)
                pool.tensor_tensor(w_lo[k][:], w_raw[k][:], w_hi[k][:].bitcast(F32), ALU.subtract).then_inc(w_split, 1)

            pool.memset(ones[:], 1.0).then_inc(consts_made, 1)
            pool.memset(ident[:], 0.0).then_inc(consts_made, 1)
            pool.wait_ge(consts_made, 2)
            pool.affine_select(out=ident[:], in_=ident[:], compare_op=ALU.not_equal, fill=1.0, base=0,
                               pattern=[[-1, P]], channel_multiplier=1).then_inc(consts_made, 1)
            pool.memset(zero[:], 0.0).then_inc(consts_made, 1)
            for g, w in enumerate(WINDOWS):
                for c in range(w - 1):
                    pool.memset(inv_cnt[:, g, c:c + 1], 1.0 / (c + 1)).then_inc(consts_made, 1)
                pool.memset(inv_cnt[:, g, w - 1:PAD], 1.0 / w).then_inc(consts_made, 1)
            pool.wait_ge(consts_made, n_consts)
            split(0, 0, 0, first=True)
            split(1, 0, 1, first=True)
            with pool.Fori(1, TILES // 2) as i:
                split(2 * i, i, 0)
                split(2 * i + 1, i, 1)

        @block.tensor
        def _(pe):
            def three(out, w_h, w_l, x_h, x_l, first, last):
                for n, (w, x) in enumerate(((w_h, x_h), (w_h, x_l), (w_l, x_h))):
                    for c in range(CH):
                        mm = pe.matmul(out[:, c, :], w, x[:, c * CW:(c + 1) * CW],
                                       start=first and n == 0, stop=last and n == 2)
                return mm

            def product(job, k, x_h, x_l, x0=0, w0=0, n=KT, ready=None):
                pe.wait_ge(evacuated, job[1])
                for b in range(n):
                    if ready is not None:
                        pe.wait_ge(ready[0], ready[1] + b)
                    col = slice((w0 + b) * P, (w0 + b + 1) * P)
                    mm = three(job_set(job[0]), w_hi[k][:, col], w_lo[k][:, col],
                               x_h[:, x0 + b, :], x_l[:, x0 + b, :], b == 0, b == n - 1)
                return mm

            def tile_ready(s):
                pe.wait_ge(w_split, s + 1)

            def norm(n, evac, ready):
                pe.wait_ge(acc_done, ready)
                pe.wait_ge(evacuated, evac)
                out = job_set(n)
                for c in range(CH):
                    mm = pe.matmul(out[:, c, :], ones[:], acc[:, c * CW:(c + 1) * CW], start=True, stop=True)
                mm.then_inc(norm_done, 1)

            pe.wait_ge(consts_made, n_consts)
            tile_ready(0)
            pe.wait_ge(evacuated, 1)
            product((J_Q0, 1), 0, h1_hi, h1_lo, ready=(h_split, 1)).then_inc(tile_done, 1)
            norm(J_NORM1, 1, KT - 1)

            def scores(n, i):
                t, h = ORDER[i // 2], i % 2
                rows = slice(h * HEAD, (h + 1) * HEAD)
                s = ps_s[i % 2]
                if t < QT:
                    nb = blocks_of(t)
                    k0 = (t + 1 - nb) * P
                    q = qT[rows, t * P:(t + 1) * P]
                    first = min(nb, 4) * P
                    mm = pe.matmul(s[:, 0:first], q, kT[rows, k0:k0 + first], start=True, stop=True)
                    if nb > 4:
                        mm = pe.matmul(s[:, first:nb * P], q, kT[rows, k0 + first:k0 + nb * P], start=True, stop=True)
                else:
                    q = qT[rows, SEQ:T]
                    pe.matmul(s[0:NEW, 0:PAST], q, ck_sb[rows, :], start=True, stop=True)
                    mm = pe.matmul(s[0:NEW, PAST:PAST + NEW], q, kT[rows, SEQ:T], start=True, stop=True)
                mm.then_inc(s_done, 1)

            def transposes(n, i):
                t = ORDER[i // 2]
                pe.wait_ge(p_done, n + 1)
                if i >= 1:
                    pe.wait_ge(pt_read, n)
                for b in range(blocks_of(t)):
                    mm = pe.transpose(ps_pt[:, b * P:(b + 1) * P], p_sb[i % 2][:, b * P:(b + 1) * P], ident[:])
                mm.then_inc(pt_done, 1)

            def values(n, i, o):
                t, h = ORDER[i // 2], i % 2
                cols = slice(h * HEAD, (h + 1) * HEAD)
                pe.wait_ge(pt_read, n + 1)
                if h == 0 and i > 0:
                    pe.wait_ge(o_read, o)
                pt = pt_sb[i % 2]
                if t < QT:
                    nb = blocks_of(t)
                    for b in range(nb):
                        mm = pe.matmul(ps_o[:, cols], pt[:, b * P:(b + 1) * P], v_tok[:, t + 1 - nb + b, cols],
                                       start=b == 0, stop=b == nb - 1)
                else:
                    for b in range(PAST // P):
                        pe.matmul(ps_o[0:NEW, cols], pt[:, b * P:b * P + NEW], cv_sb[:, b, cols],
                                  start=b == 0, stop=False)
                    mm = pe.matmul(ps_o[0:NEW, cols], pt[0:NEW, PAST:PAST + NEW], v_tok[0:NEW, QT, cols],
                                   start=False, stop=True)
                mm.then_inc(pv_done, 1)

            def turn_output(o, t):
                pe.wait_ge(o_read, o + 1)
                if t > 0:
                    pe.wait_ge(at_split, o)
                pe.transpose(ps_ot, o_tok[:], ident[:]).then_inc(ot_done, 1)

            def pair(j, last):
                tile_ready(4 * j + 1)
                product((J_PAIR, 2 + 4 * j), 1, h1_hi, h1_lo).then_inc(tile_done, 1)
                tile_ready(4 * j + 2)
                product((J_PAIR + 1, 3 + 4 * j), 0, h1_hi, h1_lo).then_inc(tile_done, 1)
                tile_ready(4 * j + 3)
                product((J_PAIR + 2, 4 + 4 * j), 1, h1_hi, h1_lo).then_inc(tile_done, 1)
                pe.wait_ge(evacuated, 5 + 4 * j)
                for b in range(OTILES):
                    m = P if b < QT else NEW
                    mm = pe.transpose(ps_vt[b // 4][0:m, (b % 4) * P:(b % 4 + 1) * P], vT[:, b * P:b * P + m], ident[:])
                mm.then_inc(vt_done, 1)
                pe.wait_ge(pair_loaded, 48 * j + 48)
                pe.wait_ge(evacuated, 6 + 4 * j)
                pe.wait_ge(v_ready, j + 1)
                for i in range(UNITS + 3):
                    n = UNITS * j + i
                    if i < UNITS:
                        scores(n, i)
                    if i >= 4 and i % 2 == 0:
                        turn_output(OTILES * j + i // 2 - 2, i // 2 - 2)
                    if 1 <= i < UNITS + 1:
                        transposes(n - 1, i - 1)
                    if 2 <= i < UNITS + 2:
                        values(n - 2, i - 2, OTILES * j + (i - 2) // 2)
                pe.wait_ge(at_split, OTILES * j + OTILES)
                if not last:
                    tile_ready(4 * j + 4)
                    product((J_PAIR + 3, 5 + 4 * j), 0, h1_hi, h1_lo).then_inc(tile_done, 1)

            with pe.Fori(0, PAIRS - 1) as j:
                pair(j, last=False)
            pair(PAIRS - 1, last=True)

            for n in range(2):
                tile_ready(S_GATE + n)
                product((J_FIRST + n, J_FIRST + n - 1), n, h1_hi, h1_lo).then_inc(tile_done, 1)
            pe.wait_ge(group_split, 1)
            for g in range(PAIRS):
                pe.wait_ge(evacuated, J_POOL + g - 1)
                pe.wait_ge(d_split, g + 1)
                three(job_set(J_POOL + g), wg_hi[:, g * P:(g + 1) * P], wg_lo[:, g * P:(g + 1) * P],
                      d_hi[g % 2][:], d_lo[g % 2][:], True, True).then_inc(pool_done, 1)

            def gates(j, odd, first=False):
                for n in range(2) if not first else ():
                    s = 3 * j + n + S_GATE
                    tile_ready(s)
                    product((J_GATE + n, J_GATE + n - 1 + 4 * j), (odd + n) % 2, h1_hi, h1_lo).then_inc(tile_done, 1)
                tile_ready(3 * j + 2 + S_GATE)
                product((J_GATE + 2, J_GATE + (2 if first else 1 + 4 * j)), odd % 2, y_hi, y_lo, n=PAIRS
                        ).then_inc(part_done, 1)
                product((J_GATE + 3, J_GATE + 2 + 4 * j), odd % 2, at_hi, at_lo, w0=PAIRS, n=PAIRS).then_inc(tile_done, 1)

            gates(0, 0, first=True)
            gates(1, 1)
            with pe.Fori(1, KT // 2) as i:
                gates(2 * i, 0)
                gates(2 * i + 1, 1)

            tile_ready(S_OUT)
            product((J_OUT, J_OUT - 1), 0, m_hi, m_lo, ready=(m_split, 1)).then_inc(tile_done, 1)
            tile_ready(S_OUT + 1)
            product((J_OUT + 1, J_OUT), 1, m_hi, m_lo).then_inc(tile_done, 1)
            with pe.Fori(1, KT // 2) as i:
                for k in range(2):
                    tile_ready(2 * i + k + S_OUT)
                    product((J_OUT + k, 2 * i + k + J_OUT - 1), k, m_hi, m_lo).then_inc(tile_done, 1)

            def up(job, s, k, **kw):
                tile_ready(s)
                product(job, k, h2_hi, h2_lo, **kw).then_inc(tile_done, 1)

            def down(job, evac, s, splits):
                pe.wait_ge(mid_split, splits)
                for m in range(KT):
                    k = m // 4
                    if m % 4 == 0:
                        tile_ready(s + k)
                    product((job + m, evac + m), k, mid_hi, mid_lo, w0=2 * (m % 4), n=2
                            ).then_inc(tile_done if m % 4 == 3 else part_done, 1)

            up((J_FFN + 1, J_FFN), S_FFN, 0, ready=(h_split, KT + 1))
            norm(J_FFN, J_FFN - 1, 2 * (KT - 1))
            up((J_FFN + 2, J_FFN + 1), S_FFN + 1, 1)
            up((J_FFN + 3, J_FFN + 2), S_FFN + 2, 0)
            up((J_FFN + 4, J_FFN + 3), S_FFN + 3, 1)
            with pe.Fori(0, GROUPS - 1) as g:
                s, e = S_FFN + 4 + 6 * g, J_GROUP - 1 + 12 * g
                up((J_GROUP, e), s, 0)
                up((J_GROUP + 1, e + 1), s + 1, 1)
                down(J_GROUP + 2, e + 2, s + 2, 2 * g + 2)
                up((J_GROUP + 10, e + 10), s + 4, 0)
                up((J_GROUP + 11, e + 11), s + 5, 1)
            down(J_DOWN, J_DOWN - 1, S_PLE - 2, FT)

            pe.wait_ge(p_split, 2)
            for m in range(KT):
                if m % 4 == 0:
                    tile_ready(S_PLE + m // 4)
                product((J_PLE + m, J_PLE + m - 1), m // 4, p_hi, p_lo, w0=2 * (m % 4), n=2
                        ).then_inc(tile_done if m % 4 == 3 else part_done, 1)
            norm(J_NORM3, J_NORM3 - 1, 3 * (KT - 1))
            pe.wait_ge(h_split, 3 * KT)
            with pe.Fori(0, KT // 2) as i:
                for k in range(2):
                    tile_ready(2 * i + k + S_PGATE)
                    product((J_PGATE + k, 2 * i + k + J_PGATE - 1), k, h2_hi, h2_lo).then_inc(tile_done, 1)
            norm(J_NORM4, J_NORM4 - 1, 4 * (KT - 1))

        @block.scalar
        def _(act):
            def g_col(which, k):
                return g_sb[:, which * KT + k:which * KT + k + 1]

            def square(x, n):
                if n % KT == 0:
                    act.activation(acc[:], x, ACT.Square).then_inc(sq_done, 1)
                else:
                    if n % KT > 1:
                        act.wait_ge(acc_done, n // KT * (KT - 1) + n % KT - 1)
                    act.activation(tmp[:, 0:T], x, ACT.Square).then_inc(sq_done, 1)

            def root(n, job, evac):
                act.wait_ge(norm_done, n)
                act.wait_ge(evacuated, evac)
                act.activation(by_chunk(rms[:]), job_set(job), ACT.Sqrt, bias=eps[:], scale=1.0 / D_MODEL
                               ).then_inc(root_done, 1)

            act.wait_ge(consts_loaded, 16)
            for k in range(KT):
                act.wait_ge(x_loaded[k], 16)
                act.activation(h1_hi[:, k, :], x_in[:, k, :], ACT.Copy, scale=g_col(0, k)).then_inc(hi_done, 1)
                square(x_in[:, k, :], k)
            act.wait_ge(line_made, 1)
            act.dma_start(line_dram, line[0:2 * PAIRS, None, :].broadcast_to([2 * PAIRS, P, LINE])
                          ).then_inc(line_stored, 16)
            root(1, J_NORM1, 1)

            def exponentials(n, i):
                t = ORDER[i // 2]
                m = P if t < QT else NEW
                nk = blocks_of(t) * P if t < QT else PAST + NEW
                act.wait_ge(s_read, n + 1)
                if i >= 2:
                    act.wait_ge(pt_done, n - 1)
                c = i % 4
                if i >= 4:
                    act.wait_ge(inv_done, n - 3)
                act.activation(p_sb[i % 2][0:m, 0:nk], s_sb[i % 2][0:m, 0:nk], ACT.Exp, bias=nmax[0:m, c:c + 1],
                               scale=-1.0, accum_out=rsum[0:m, c:c + 1]).then_inc(p_done, 1)

            def read_output(j, u):
                o = OTILES * j + u
                m = P if ORDER[u] < QT else NEW
                act.wait_ge(pv_done, UNITS * j + 2 * u + 2)
                act.wait_ge(inv_done, UNITS * j + 2 * u + 2)
                if u > 0:
                    act.wait_ge(ot_done, o)
                for h in range(2):
                    c = (2 * u + h) % 4
                    ins = act.activation(o_tok[0:m, h * HEAD:(h + 1) * HEAD], ps_o[0:m, h * HEAD:(h + 1) * HEAD],
                                         ACT.Copy, scale=rinv[0:m, c:c + 1])
                ins.then_inc(o_read, 1)

            def output_hi(j, u):
                t = ORDER[u]
                m = P if t < QT else NEW
                act.wait_ge(ot_done, OTILES * j + u + 1)
                act.activation(at_hi[:, j, t * P:t * P + m], ps_ot[:, 0:m], ACT.Copy).then_inc(at_hi_done, 1)

            def pair(j, last):
                act.wait_ge(evacuated, J_PAIR + 1 + 4 * j)
                act.dma_start(o_k[j], kT[:, SEQ - PAST:T]).then_inc(kv_stored, 16)
                act.wait_ge(evacuated, J_PAIR + 2 + 4 * j)
                act.dma_start(o_v[j], vT[:, SEQ - PAST:T]).then_inc(kv_stored, 16)
                act.wait_ge(vt_done, j + 1)
                for k in range(2):
                    act.activation(v_tok[:, 4 * k:4 * k + 4, :].rearrange("p a b -> p (a b)"), ps_vt[k], ACT.Copy)
                act.activation(v_tok[0:NEW, QT, :], ps_vt[2][0:NEW, :], ACT.Copy).then_inc(v_ready, 1)
                for i in range(UNITS + 3):
                    if i < UNITS:
                        exponentials(UNITS * j + i, i)
                    if i >= 3 and i % 2 == 1:
                        read_output(j, (i - 3) // 2)
                    if i >= 4 and i % 2 == 0:
                        output_hi(j, (i - 4) // 2)

            with act.Fori(0, PAIRS - 1) as j:
                pair(j, last=False)
            pair(PAIRS - 1, last=True)

            act.wait_ge(evacuated, J_PAIR + 4 * PAIRS - 1)
            act.dma_start(o_pool_p, u_row[:, :, PAD + SEQ - HIST:PAD + SEQ]).then_inc(pool_stored, 16)
            act.dma_start(o_pool_s, u_row[:, :, UW - HIST:UW]).then_inc(pool_stored, 16)
            act.wait_ge(group_loaded, 16)
            act.activation(wg_hi[:], wg_raw[:], ACT.Copy).then_inc(group_hi, 1)

            def difference_hi(g):
                act.wait_ge(d_ready, g + 1)
                if g > 1:
                    act.wait_ge(pool_done, g - 1)
                act.activation(d_hi[g % 2][:, 0:SEQ], u_row[:, g, PAD:PAD + SEQ], ACT.Copy)
                act.activation(d_hi[g % 2][:, SEQ:T], u_row[:, g, SAMPLE_U:UW], ACT.Copy).then_inc(d_hi_done, 1)

            def pooled_hi(g):
                act.wait_ge(pool_done, g + 1)
                act.activation(by_chunk(y_hi[:, g, :]), job_set(J_POOL + g), ACT.Copy, scale=pool_sc[:, g:g + 1]
                               ).then_inc(y_hi_done, 1)

            def sigmoids(j, evac):
                act.wait_ge(evacuated, evac)
                act.activation(tmp[:, 0:T], tmp[:, 0:T], ACT.Sigmoid, bias=gate_b[:, bass.ds(j, 1)]
                               ).then_inc(gate_out, 1)
                act.wait_ge(evacuated, evac + 1)
                act.activation(acc[:], acc[:], ACT.Sigmoid, bias=gate_b[:, bass.ds(j + KT, 1)]
                               ).then_inc(gate_out, 1)

            difference_hi(0)
            difference_hi(1)
            for g in range(PAIRS):
                pooled_hi(g)
                if g + 2 < PAIRS:
                    difference_hi(g + 2)
            sigmoids(0, J_FIRST + 1)
            with act.Fori(1, KT) as j:
                sigmoids(j, J_GATE + 1 + 4 * j)

            act.wait_ge(tile_done, S_OUT)
            act.wait_ge(merged_ready, KT)
            for k in range(KT):
                act.activation(m_hi[:, k, :], merged[:, k, :], ACT.Copy).then_inc(m_hi_done, 1)
            act.wait_ge(m_split, KT)
            for k in range(KT):
                act.dma_start(x_res[:, k, :], xT[k]).then_inc(x_again[k], 16)
            for k in range(KT):
                act.wait_ge(evacuated, J_OUT + k + 1)
                act.activation(h2_hi[:, k, :], x_res[:, k, :], ACT.Copy, scale=g_col(1, k)).then_inc(hi_done, 1)
                square(x_res[:, k, :], KT + k)
            act.wait_ge(tile_done, S_FFN)
            act.dma_start(p_raw[:], pT).then_inc(p_loaded, 16)
            root(2, J_FFN, J_FFN)

            def ffn_tile(f, slot, evac, downs):
                act.wait_ge(evacuated, evac)
                act.activation(conv[:], a_row[:, 0:CWID], ACT.Identity, bias=dw[:, bass.ds(f + 3 * FT, 1)],
                               scale=dw[:, bass.ds(f, 1)]).then_inc(conv0_done, 1)
                act.activation(conv_new[:, f, 0:2], a_row[:, SEQ:SEQ + 2], ACT.Copy)
                act.activation(conv_new[:, f, 2:4], a_row[:, AW - 2:AW], ACT.Copy).then_inc(conv_kept, 1)
                act.wait_ge(conv_done, f + 1)
                act.activation(gel[:], conv[:], ACT.Gelu_apprx_tanh).then_inc(gelu_done, 1)
                act.wait_ge(mid_ready, f + 1)
                if downs is not None:
                    act.wait_ge(tile_done, downs)
                act.activation(mid_hi[:, slot, :], mid[:], ACT.Copy).then_inc(mid_hi_done, 1)

            ffn_tile(0, 0, J_FFN + 2, None)
            ffn_tile(1, 1, J_FFN + 4, None)
            act.wait_ge(p_loaded, 16)
            for k in range(2):
                act.activation(p_hi[:, k, :], p_raw[:, k, :], ACT.Copy).then_inc(p_hi_done, 1)
            with act.Fori(1, GROUPS) as g:
                for slot in range(2):
                    ffn_tile(2 * g + slot, slot, 12 * g + J_GROUP - 11 + 10 * slot, 6 * g + S_FFN + 2)
            act.wait_ge(conv_kept, FT)
            act.dma_start(o_conv, conv_new[:]).then_inc(stored, 16)
            for k in range(KT):
                act.wait_ge(evacuated, J_DOWN + k + 1)
                act.activation(h2_hi[:, k, :], x_res[:, k, :], ACT.Copy, scale=g_col(2, k)).then_inc(hi_done, 1)
            for k in range(KT):
                square(x_res[:, k, :], 2 * KT + k)
            root(3, J_NORM3, J_NORM3)
            for k in range(KT):
                act.wait_ge(evacuated, J_PGATE + k + 1)
                act.activation(gate_sb[:], gate_sb[:], ACT.Sigmoid).then_inc(gate_out, 1)
                act.wait_ge(x4_ready, k + 1)
                square(x_res[:, k, :], 3 * KT + k)
            root(4, J_NORM4, J_NORM4)
            for k in range(KT):
                act.wait_ge(y_ready, k + 1)
                act.dma_start(o_y[k], x_res[:, k, :]).then_inc(stored, 16)
            act.wait_ge(kv_stored, 32 * PAIRS)
            act.wait_ge(pool_stored, 32)
            act.wait_ge(stored, 16 * (1 + KT))

        @block.vector
        def _(dve):
            def g_col(which, k):
                return g_sb[:, which * KT + k:which * KT + k + 1]

            def input_lo(dst_hi, dst_lo, x, which, k, n):
                dve.wait_ge(hi_done, n + 1)
                dve.scalar_tensor_tensor(out=dst_lo[:, k, :], in0=x[:, k, :], scalar=g_col(which, k),
                                         in1=dst_hi[:, k, :].bitcast(F32), op0=ALU.mult, op1=ALU.subtract
                                         ).then_inc(h_split, 1)

            def add_squares(n):
                if n % KT:
                    dve.wait_ge(sq_done, n + 1)
                    if n % KT > 1:
                        dve.wait_ge(acc_done, n // KT * (KT - 1) + n % KT - 1)
                    dve.tensor_tensor(acc[:], acc[:], tmp[:, 0:T], ALU.add).then_inc(acc_done, 1)

            def invert_rms(n, job):
                dve.wait_ge(root_done, n)
                dve.memset(gap[:], 0.0).then_inc(evacuated, 1)
                dve.reciprocal(rms[:], rms[:]).then_inc(rms_ready, 1)
                dve.wait_ge(rms_ready, n)
                dve.wait_ge(evacuated, job + 1)

            def scaled(dst, job):
                dve.tensor_tensor(by_chunk(dst), job_set(job), by_chunk(rms[:]), ALU.mult).then_inc(evacuated, 1)

            def scaled_row(row, start, sample, job):
                s = job_set(job)
                rest = SEQ - 2 * CW
                dve.tensor_tensor(row[:, start:start + 2 * CW].rearrange("p (c n) -> p c n", c=2), s[:, 0:2, :],
                                  rms[:, 0:2 * CW].rearrange("p (c n) -> p c n", c=2), ALU.mult)
                dve.tensor_tensor(row[:, start + 2 * CW:start + SEQ], s[:, 2, 0:rest], rms[:, 2 * CW:SEQ], ALU.mult)
                dve.tensor_tensor(row[:, sample:sample + NEW], s[:, 2, rest:CW], rms[:, SEQ:T], ALU.mult
                                  ).then_inc(evacuated, 1)

            dve.memset(eps[:], EPS).then_inc(evacuated, 1)
            far = slice(0, LINE - N_REL)
            dve.memset(line[0:2 * PAIRS, far], 0.0).then_inc(link, 1)
            dve.wait_ge(line_loaded, 16)
            dve.tensor_scalar(line[0:2 * PAIRS, LINE - N_REL:LINE], line[0:2 * PAIRS, LINE - N_REL:LINE], 1 / SCALE,
                              None, ALU.mult).then_inc(link, 1)
            dve.wait_ge(link, 2)
            dve.tensor_scalar(line[0:2 * PAIRS, far], line[0:2 * PAIRS, far],
                              line[0:2 * PAIRS, LINE - N_REL:LINE - N_REL + 1], None, ALU.add).then_inc(line_made, 1)

            dve.wait_ge(consts_loaded, 16)
            for k in range(KT):
                input_lo(h1_hi, h1_lo, x_in, 0, k, k)
                add_squares(k)
            dve.wait_ge(sq_done, KT)
            dve.wait_ge(h_split, KT)
            dve.memset(u_row[:, :, 0:PAD], 0.0)
            dve.memset(u_row[:, :, PAD + SEQ:PAD + SEQ + 1], 0.0).then_inc(link, 1)
            invert_rms(1, J_NORM1)
            dve.wait_ge(tile_done, 1)
            scaled(qT[:], J_Q0)

            def read_scores(n, i):
                t = ORDER[i // 2]
                m = P if t < QT else NEW
                dve.wait_ge(s_done, n + 1)
                if i >= 2:
                    dve.wait_ge(p_done, n - 1)
                if t < QT:
                    nk = blocks_of(t) * P
                    bias = bias_sb[0:m, i % 2, BAND - nk:BAND]
                else:
                    nk = PAST + NEW
                    bias = bias_sb[0:m, i % 2, 0:nk]
                dve.memset(gap[0:m, i % 4:i % 4 + 1], 0.0)
                dve.tensor_tensor_reduce(out=s_sb[i % 2][0:m, 0:nk], in0=ps_s[i % 2][0:m, 0:nk], in1=bias,
                                         scale=-SCALE, scalar=BIG, op0=ALU.add, op1=ALU.min,
                                         accum_out=nmax[0:m, i % 4:i % 4 + 1]).then_inc(s_read, 1)

            def invert_sum(j, n, i):
                m = P if ORDER[i // 2] < QT else NEW
                dve.wait_ge(p_done, n + 1)
                if i >= 4:
                    dve.wait_ge(o_read, OTILES * j + i // 2 - 1)
                dve.reciprocal(rinv[0:m, i % 4:i % 4 + 1], rsum[0:m, i % 4:i % 4 + 1]).then_inc(inv_done, 1)

            def read_transposes(n, i):
                t = ORDER[i // 2]
                dve.wait_ge(pt_done, n + 1)
                if i >= 2:
                    dve.wait_ge(pv_done, n - 1)
                nk = blocks_of(t) * P
                dve.tensor_copy(pt_sb[i % 2][:, 0:nk], ps_pt[:, 0:nk]).then_inc(pt_read, 1)

            def output_lo(j, u):
                t = ORDER[u]
                m = P if t < QT else NEW
                dve.wait_ge(at_hi_done, OTILES * j + u + 1)
                dve.tensor_tensor(at_lo[:, j, t * P:t * P + m], ps_ot[:, 0:m],
                                  at_hi[:, j, t * P:t * P + m].bitcast(F32), ALU.subtract).then_inc(at_split, 1)

            def pair(j, last):
                dve.wait_ge(tile_done, 4 * j + 2)
                scaled(kT[:], J_PAIR)
                dve.wait_ge(tile_done, 4 * j + 3)
                scaled(vT[:], J_PAIR + 1)
                dve.wait_ge(tile_done, 4 * j + 4)
                scaled_row(u_row[:, j, :], PAD, SAMPLE_U, J_PAIR + 2)
                dve.wait_ge(pair_loaded, 48 * j + 48)
                dve.memset(bias_sb[0:CHUNK, :, BAND - CHUNK:BAND], MASKED).then_inc(mask_set, 1)
                dve.memset(bias_sb[CHUNK:P, :, 0:CHUNK], MASKED).then_inc(mask_set, 1)
                dve.wait_ge(mask_set, 2 * j + 2)
                for i in range(UNITS + 4):
                    if i < UNITS:
                        read_scores(UNITS * j + i, i)
                    if 1 <= i < UNITS + 1:
                        invert_sum(j, UNITS * j + i - 1, i - 1)
                        read_transposes(UNITS * j + i - 1, i - 1)
                    if i >= 5 and i % 2 == 1:
                        output_lo(j, (i - 5) // 2)
                dve.wait_ge(kv_stored, 32 * j + 32)
                if not last:
                    dve.wait_ge(tile_done, 4 * j + 5)
                    scaled(qT[:], J_PAIR + 3)

            with dve.Fori(0, PAIRS - 1) as j:
                pair(j, last=False)
            pair(PAIRS - 1, last=True)

            dve.wait_ge(group_loaded, 16)
            dve.wait_ge(group_hi, 1)
            dve.tensor_tensor(wg_lo[:], wg_raw[:], wg_hi[:].bitcast(F32), ALU.subtract).then_inc(group_split, 1)
            dve.wait_ge(pool_hist_loaded, 16 * PAIRS)
            dve.wait_ge(consts_made, n_consts)
            dve.wait_ge(evacuated, J_FIRST)
            chain = 3
            dve.wait_ge(link, chain)

            def average(g, chain):
                w = WINDOWS[g]
                u = u_row[:, g, :]
                steps = w.bit_length() - 1
                src, width = u, 1
                for step in range(steps):
                    dst = (win if (steps - step) % 2 else part)[:]
                    lo = 2 * width - 1
                    dve.tensor_tensor(dst[:, lo:UW], src[:, lo:UW], src[:, lo - width:UW - width], ALU.add
                                      ).then_inc(link, 1)
                    chain += 1
                    dve.wait_ge(link, chain)
                    src, width = dst, 2 * width
                dve.tensor_tensor(part[:, 0:PAD], win[:, PAD:2 * PAD], inv_cnt[:, g, :], ALU.mult).then_inc(link, 1)
                chain += 1
                dve.wait_ge(link, chain)
                dve.tensor_tensor(u[:, PAD:2 * PAD], part[:, 0:PAD], u[:, PAD:2 * PAD], ALU.subtract)
                for lo, hi in ((2 * PAD, PAD + SEQ), (SAMPLE_U, UW)):
                    ins = dve.scalar_tensor_tensor(out=u[:, lo:hi], in0=win[:, lo:hi], scalar=1.0 / w,
                                                   in1=u[:, lo:hi], op0=ALU.mult, op1=ALU.subtract)
                ins.then_inc(d_ready, 1)
                dve.wait_ge(d_ready, g + 1)
                return chain

            def difference_lo(g):
                dve.wait_ge(d_hi_done, g + 1)
                for dst, src in ((slice(0, SEQ), slice(PAD, PAD + SEQ)), (slice(SEQ, T), slice(SAMPLE_U, UW))):
                    ins = dve.tensor_tensor(d_lo[g % 2][:, dst], u_row[:, g, src], d_hi[g % 2][:, dst].bitcast(F32),
                                            ALU.subtract)
                ins.then_inc(d_split, 1)

            dve.wait_ge(pool_stored, 32)
            chain = average(0, chain)
            difference_lo(0)
            chain = average(1, chain)
            difference_lo(1)
            dve.wait_ge(tile_done, S_GATE + 1)
            scaled(tmp[:, 0:T], J_FIRST)
            chain = average(2, chain)
            chain = average(3, chain)
            dve.wait_ge(tile_done, S_GATE + 2)
            scaled(acc[:], J_FIRST + 1)
            for g in range(PAIRS):
                dve.wait_ge(y_hi_done, g + 1)
                dve.scalar_tensor_tensor(out=by_chunk(y_lo[:, g, :]), in0=job_set(J_POOL + g),
                                         scalar=pool_sc[:, g:g + 1], in1=by_chunk(y_hi[:, g, :].bitcast(F32)),
                                         op0=ALU.mult, op1=ALU.subtract).then_inc(evacuated, 1)
                if g + 2 < PAIRS:
                    difference_lo(g + 2)

            def merge(j, first=False):
                if not first:
                    dve.wait_ge(tile_done, 3 * j + S_GATE + 1)
                    scaled(tmp[:, 0:T], J_GATE)
                    dve.wait_ge(tile_done, 3 * j + S_GATE + 2)
                    scaled(acc[:], J_GATE + 1)
                dve.wait_ge(part_done, j + 1)
                dve.wait_ge(gate_out, 2 * j + 1)
                dve.tensor_tensor(by_chunk(tmp[:, 0:T]), job_set(J_GATE + 2), by_chunk(tmp[:, 0:T]), ALU.mult
                                  ).then_inc(evacuated, 1)
                dve.wait_ge(tile_done, 3 * j + S_GATE + 3)
                dve.wait_ge(gate_out, 2 * j + 2)
                dve.tensor_tensor(by_chunk(acc[:]), job_set(J_GATE + 3), by_chunk(acc[:]), ALU.mult
                                  ).then_inc(evacuated, 1)
                dve.wait_ge(evacuated, 4 * j + J_GATE + 4)
                dve.tensor_tensor(merged[:, j, :], tmp[:, 0:T], acc[:], ALU.add).then_inc(merged_ready, 1)
                dve.wait_ge(merged_ready, j + 1)

            merge(0, first=True)
            with dve.Fori(1, KT) as j:
                merge(j)
            for k in range(KT):
                dve.wait_ge(m_hi_done, k + 1)
                dve.tensor_tensor(m_lo[:, k, :], merged[:, k, :], m_hi[:, k, :].bitcast(F32), ALU.subtract
                                  ).then_inc(m_split, 1)

            def add_to_residual(m, job):
                dve.tensor_tensor(by_chunk(x_res[:, m, :]), job_set(job), by_chunk(x_res[:, m, :]), ALU.add
                                  ).then_inc(evacuated, 1)

            for k in range(KT):
                dve.wait_ge(tile_done, S_OUT + k + 1)
                dve.wait_ge(x_again[k], 16)
                add_to_residual(k, J_OUT + k)
                dve.wait_ge(evacuated, J_OUT + k + 1)
                input_lo(h2_hi, h2_lo, x_res, 1, k, KT + k)
                add_squares(KT + k)
            dve.memset(a_row[:, 0:2], 0.0).then_inc(link, 1)
            invert_rms(2, J_FFN)
            dve.wait_ge(consts_loaded, 16 * 5)

            def ffn_a(f, s, job, evac, first=False):
                dve.wait_ge(tile_done, s + 1)
                if not first:
                    dve.wait_ge(conv_kept, f)
                    dve.wait_ge(conv_done, f)
                dve.tensor_copy(a_row[:, SEQ + 2:SEQ + 4], conv_hist[:, f, :])
                scaled_row(a_row, 2, SAMPLE_A, job)
                dve.wait_ge(evacuated, evac + 1)
                dve.wait_ge(conv0_done, f + 1)
                dve.scalar_tensor_tensor(out=conv[:], in0=a_row[:, 1:1 + CWID], scalar=dw[:, bass.ds(f + FT, 1)],
                                         in1=conv[:], op0=ALU.mult, op1=ALU.add).then_inc(conv1_done, 1)
                dve.wait_ge(conv1_done, f + 1)
                dve.scalar_tensor_tensor(out=conv[:], in0=a_row[:, 2:2 + CWID], scalar=dw[:, bass.ds(f + 2 * FT, 1)],
                                         in1=conv[:], op0=ALU.mult, op1=ALU.add).then_inc(conv_done, 1)

            def ffn_b(f, s, job, evac, first=False):
                dve.wait_ge(tile_done, s + 1)
                scaled(b_row[:], job)
                dve.wait_ge(evacuated, evac + 1)
                dve.wait_ge(gelu_done, f + 1)
                if not first:
                    dve.wait_ge(mid_split, f)
                dve.tensor_tensor(mid[:, 0:SEQ], gel[:, 0:SEQ], b_row[:, 0:SEQ], ALU.mult)
                dve.tensor_tensor(mid[:, SEQ:T], gel[:, SEQ + 2:CWID], b_row[:, SEQ:T], ALU.mult).then_inc(mid_ready, 1)

            def ffn_lo(f, slot):
                dve.wait_ge(mid_ready, f + 1)
                dve.wait_ge(mid_hi_done, f + 1)
                dve.tensor_tensor(mid_lo[:, slot, :], mid[:], mid_hi[:, slot, :].bitcast(F32), ALU.subtract
                                  ).then_inc(mid_split, 1)

            def down_ready(m, s, parts):
                if m % 4 == 3:
                    dve.wait_ge(tile_done, s + m // 4 + 1)
                else:
                    dve.wait_ge(part_done, parts + 3 * (m // 4) + m % 4 + 1)

            ffn_a(0, S_FFN, J_FFN + 1, J_FFN + 1, first=True)
            ffn_b(0, S_FFN + 1, J_FFN + 2, J_FFN + 2, first=True)
            ffn_lo(0, 0)
            ffn_a(1, S_FFN + 2, J_FFN + 3, J_FFN + 3)
            ffn_b(1, S_FFN + 3, J_FFN + 4, J_FFN + 4)
            ffn_lo(1, 1)
            for k in range(2):
                dve.wait_ge(p_hi_done, k + 1)
                dve.tensor_tensor(p_lo[:, k, :], p_raw[:, k, :], p_hi[:, k, :].bitcast(F32), ALU.subtract
                                  ).then_inc(p_split, 1)
            with dve.Fori(1, GROUPS) as g:
                s = 6 * g + S_FFN - 2
                e = 12 * g + J_GROUP - 12
                f = 2 * g
                ffn_a(f, s, J_GROUP, e)
                ffn_b(f, s + 1, J_GROUP + 1, e + 1)
                for m in range(KT):
                    down_ready(m, s + 2, 6 * g + KT - 6)
                    add_to_residual(m, J_GROUP + 2 + m)
                dve.wait_ge(evacuated, e + 10)
                ffn_lo(f, 0)
                ffn_a(f + 1, s + 4, J_GROUP + 10, e + 10)
                ffn_b(f + 1, s + 5, J_GROUP + 11, e + 11)
                ffn_lo(f + 1, 1)
            dve.wait_ge(evacuated, J_DOWN)
            for k in range(KT):
                down_ready(k, S_PLE - 2, KT + 6 * (GROUPS - 1))
                add_to_residual(k, J_DOWN + k)
                if k > 0:
                    dve.wait_ge(evacuated, J_DOWN + k)
                    input_lo(h2_hi, h2_lo, x_res, 2, k - 1, 2 * KT + k - 1)
            dve.wait_ge(evacuated, J_DOWN + KT)
            input_lo(h2_hi, h2_lo, x_res, 2, KT - 1, 3 * KT - 1)

            for m in range(KT):
                down_ready(m, S_PLE, KT + 6 * GROUPS)
                dve.tensor_copy(by_chunk(ple[:, m, :]), job_set(J_PLE + m)).then_inc(evacuated, 1)
                add_squares(2 * KT + m)
            invert_rms(3, J_NORM3)
            for k in range(KT):
                dve.wait_ge(tile_done, S_PGATE + k + 1)
                if k > 0:
                    dve.wait_ge(x4_ready, k)
                scaled(gate_sb[:], J_PGATE + k)
                dve.wait_ge(gate_out, 2 * KT + k + 1)
                dve.tensor_tensor(gate_sb[:], gate_sb[:], ple[:, k, :], ALU.mult).then_inc(gated, 1)
                dve.wait_ge(gated, k + 1)
                dve.tensor_tensor(x_res[:, k, :], x_res[:, k, :], gate_sb[:], ALU.add).then_inc(x4_ready, 1)
                add_squares(3 * KT + k)
            invert_rms(4, J_NORM4)
            dve.wait_ge(x4_ready, KT)
            for k in range(KT):
                dve.scalar_tensor_tensor(out=x_res[:, k, :], in0=x_res[:, k, :], scalar=g_col(3, k), in1=rms[:],
                                         op0=ALU.mult, op1=ALU.mult).then_inc(y_ready, 1)


def blocks(w):
    k, n = w.shape
    return w.reshape(k // P, P, n // P, P).transpose(2, 1, 0, 3)


def weight_stream(i):
    w_in = blocks(i["w_in"][0])
    u, q, k, v = (w_in[n * PAIRS:(n + 1) * PAIRS] for n in range(4))
    gates = w_in[4 * PAIRS:]
    out = []
    for j in range(PAIRS):
        out += [q[j], k[j], v[j], u[j]]
    proj = np.concatenate([blocks(i["w_pool_proj"][0]), blocks(i["w_attn_proj"][0])], axis=2)
    for j in range(KT):
        out += [gates[j], gates[KT + j], proj[j]]
    out += list(blocks(i["w_out"][0]))
    up = blocks(i["w_up"][0])
    down = blocks(i["w_down"][0])

    def two_deep(w, g):
        part = w[:, :, 2 * g:2 * g + 2, :]
        return [part[4 * n:4 * n + 4].transpose(1, 0, 2, 3).reshape(P, 8, P) for n in range(2)]

    for g in range(GROUPS):
        for f in (2 * g, 2 * g + 1):
            out += [up[f], up[FT + f]]
            if f == 2 * g and g > 0:
                out += two_deep(down, g - 1)
    out += two_deep(down, GROUPS - 1)
    out += two_deep(blocks(i["w_ple"][0]), 0)
    out += list(blocks(i["w_ple_gate"][0]))
    return np.ascontiguousarray(np.stack(out).reshape(TILES, P, KT * P))


def columns(v):
    return np.reshape(v, (-1, P)).T


def kernel(**inputs):
    import concourse.bacc as bacc
    from concourse.bass_utils import run_bass_kernel_spmd

    i = {k: np.asarray(v) for k, v in inputs.items()}

    def frames(prompt, sample):
        both = np.concatenate([prompt.reshape(SEQ, -1), sample.reshape(NEW, -1)])
        return both.T.reshape(-1, P, T)

    c = np.ascontiguousarray
    ins = {
        "xT": c(frames(i["x_prompt"], i["x_sample"])),
        "pT": c(frames(i["p_prompt"], i["p_sample"]).transpose(1, 0, 2)),
        "w_stream": weight_stream(i),
        "w_group": c(i["w_pool_grp"][0].transpose(1, 0, 2).reshape(P, PAIRS * P)),
        "relr": c(i["rel_bias"][0][:, ::-1]),
        "g_cols": c(np.concatenate([columns(i[n]) for n in ("g_mix", "g_ffn", "g_ple", "g_final")], axis=1)),
        "bias_cols": c(columns(i["b_gate"])),
        "pool_cols": c(columns(i["pool_scale"])),
        "dw_cols": c(np.concatenate([columns(i["w_dw"]), columns(i["b_dw"])], axis=1)),
        "ckT": c(i["cache_k"].reshape(PAST, PAIRS, P).transpose(1, 2, 0)),
        "cv": c(i["cache_v"].reshape(PAST // P, P, PAIRS, P).transpose(2, 1, 0, 3)),
        "cpoolT": c(i["cache_pool"][0, 0].T.reshape(PAIRS, P, HIST)),
        "cconvT": c(i["cache_ffn_conv"][0, 0].T.reshape(FT, P, 2).transpose(1, 0, 2)),
    }
    outs = {
        "o_y": (KT, P, T),
        "o_pool_p": (P, PAIRS, HIST),
        "o_pool_s": (P, PAIRS, HIST),
        "o_k": (PAIRS, P, PAST + NEW),
        "o_v": (PAIRS, P, PAST + NEW),
        "o_conv": (P, FT, 4),
    }
    nc = bacc.Bacc("TRN2", target_bir_lowering=False, num_devices=1, dynamic_dma_scratch_size=1024)
    aps = [nc.dram_tensor(n, a.shape, F32, kind="ExternalInput").ap() for n, a in ins.items()]
    aps += [nc.dram_tensor(n, s, F32, kind="ExternalOutput").ap() for n, s in outs.items()]
    build(nc, *aps)
    r = run_bass_kernel_spmd(nc, [ins], core_ids=[0]).results[0]

    y = np.asarray(r["o_y"]).reshape(D_MODEL, T).T
    pool_p, pool_s = (np.asarray(r[n]).transpose(2, 1, 0).reshape(1, 1, HIST, PAIRS * P) for n in ("o_pool_p", "o_pool_s"))
    kv = [np.asarray(r[n]).transpose(2, 0, 1).reshape(PAST + NEW, 2 * PAIRS, HEAD) for n in ("o_k", "o_v")]
    conv = np.asarray(r["o_conv"]).transpose(2, 1, 0).reshape(4, FF)
    return (c(y[None, :SEQ]), c(y[None, SEQ:]), c(pool_p),
            c(kv[0][None, None, :PAST]), c(kv[1][None, None, :PAST]), c(conv[None, None, 0:2]),
            c(pool_s), c(kv[0][None, None, PAST:]), c(kv[1][None, None, PAST:]), c(conv[None, None, 2:4]))
```
